# Optimizing a Trainium2 kernel written in Bass

```python
import jax, jax.numpy as jnp
from jax import lax
import numpy as np

D_MODEL = 1024
BATCH = 1
SEQ = 1024
DEPTH = 2
DEC_BATCH = 8
DEC_SEQ = 4
PAST_LEN = 2048
PAGE_SIZE = 128

D_MIX = D_MODEL
H_A = 4
W_A = (3 * D_MIX) // 8
DV_A = W_A // H_A
DK_A = DV_A // 2
CHUNK_A = 128
POOL_WINDOWS = (2, 4, 8, 16)
G_B = 4
W_B = D_MIX // 4
CG_B = W_B // G_B
POOL_HIST = 15
DH_C = 64
W_C = D_MIX - W_A - W_B
H_C = W_C // DH_C
Q_BLOCK = 128
D_FF = 4 * D_MODEL
EPS = 1e-6
FGATE_BIAS_C = 3.0

IN_SIZES = (H_A * DK_A, H_A * DK_A, W_A, H_A, H_A, W_A, W_B, W_C, W_C, W_C, H_C)
N_IN = H_A * DK_A * 2 + W_A * 2 + H_A * 2 + W_B + W_C * 3 + H_C

kernel_name = "hymba_mlstm_pool_fox_decode_step"

def rmsnorm(x, g):
    xf = x.astype(jnp.float32)
    return xf * lax.rsqrt(jnp.mean(xf * xf, axis=-1, keepdims=True) + EPS) * g.astype(jnp.float32)

def split_cols(p):
    out = []
    o = 0
    for n in IN_SIZES:
        out.append(p[..., o:o + n])
        o += n
    return out

def col_offset(i):
    return sum(IN_SIZES[:i])

def mlstm(q, k, v, ig, fg, C0, n0, m0):
    B, T, H, DK = q.shape
    L = CHUNK_A if T % CHUNK_A == 0 else T
    NC = T // L

    def chunks(a):
        a = a.reshape((B, NC, L) + a.shape[2:])
        return jnp.swapaxes(jnp.moveaxis(a, 1, 0), 2, 3)

    causal = jnp.tril(jnp.ones((L, L), dtype=bool))

    def step(carry, inp):
        C, n, m = carry
        qc, kc, vc, ic, fc = inp
        bc = jnp.cumsum(jax.nn.log_sigmoid(fc), axis=-1)
        D = jnp.where(causal, bc[..., :, None] - bc[..., None, :] + ic[..., None, :], -jnp.inf)
        inter = bc + m[..., None]
        mt = jnp.maximum(inter, jnp.max(D, axis=-1))
        a = jnp.exp(inter - mt)
        S = jnp.einsum("bhtd,bhsd->bhts", qc, kc) * jnp.exp(D - mt[..., None])
        num = a[..., None] * jnp.einsum("bhvd,bhtd->bhtv", C, qc) + jnp.einsum("bhts,bhsv->bhtv", S, vc)
        den = a * jnp.einsum("bhd,bhtd->bht", n, qc) + jnp.sum(S, axis=-1)
        h = num / jnp.maximum(jnp.abs(den), jnp.exp(-mt))[..., None]
        m_new = mt[..., -1]
        g = jnp.exp(D[..., -1, :] - m_new[..., None])
        a_last = jnp.exp(inter[..., -1] - m_new)
        C_new = a_last[..., None, None] * C + jnp.einsum("bhs,bhsv,bhsd->bhvd", g, vc, kc)
        n_new = a_last[..., None] * n + jnp.einsum("bhs,bhsd->bhd", g, kc)
        return (C_new, n_new, m_new), h

    (C1, n1, m1), hs = lax.scan(step, (C0, n0, m0),
                                (chunks(q), chunks(k), chunks(v), chunks(ig), chunks(fg)))
    hs = jnp.moveaxis(jnp.swapaxes(hs, 2, 3), 0, 1).reshape(B, T, H, v.shape[-1])
    return hs, C1, n1, m1

def pool_mix(u, hist, pos0, w_pool, s_pool):
    B, T, _ = u.shape
    z = jnp.concatenate([hist.astype(jnp.float32), u.astype(jnp.float32)], axis=1)
    S = jnp.concatenate([jnp.zeros((B, 1, W_B), jnp.float32), jnp.cumsum(z, axis=1)], axis=1)
    n_avail = (pos0 + jnp.arange(T) + 1).astype(jnp.float32)
    outs = []
    for g, w in enumerate(POOL_WINDOWS):
        sl = slice(g * CG_B, (g + 1) * CG_B)
        wsum = S[:, POOL_HIST + 1:POOL_HIST + 1 + T, sl] - S[:, POOL_HIST + 1 - w:POOL_HIST + 1 - w + T, sl]
        cnt = jnp.minimum(jnp.float32(w), n_avail)[None, :, None]
        outs.append(wsum / cnt - z[:, POOL_HIST:, sl])
    y = jnp.stack(outs, axis=2)
    y = jnp.einsum("btgc,gcd->btgd", y, w_pool).reshape(B, T, W_B) * s_pool
    return y, z[:, -POOL_HIST:]

def fox_block(q, Fq, qpos, k, v, Ft, kpos):
    s = jnp.einsum("bqhd,bshd->bhqs", q, k) * (DH_C ** -0.5)
    s = s + jnp.swapaxes(Fq, 1, 2)[..., None] - Ft[:, :, None, :]
    s = jnp.where(qpos[:, None] >= kpos[None, :], s, -jnp.inf)
    p = jax.nn.softmax(s, axis=-1)
    return jnp.einsum("bhqs,bshd->bqhd", p, v)

def fox_prompt(q, k, v, lf):
    B, T, H, dh = q.shape
    QB = min(Q_BLOCK, T)
    nb = T // QB
    F = jnp.cumsum(lf, axis=1)
    Ft = jnp.swapaxes(F, 1, 2)
    kpos = jnp.arange(T)
    qb = jnp.swapaxes(q.reshape(B, nb, QB, H, dh), 0, 1)
    Fb = jnp.swapaxes(F.reshape(B, nb, QB, H), 0, 1)
    starts = jnp.arange(nb) * QB
    out = lax.map(lambda a: fox_block(a[0], a[1], a[2] + jnp.arange(QB), k, v, Ft, kpos), (qb, Fb, starts))
    return jnp.swapaxes(out, 0, 1).reshape(B, T, H, dh)

def fox_sample(q, k, v, lf, cache_k, cache_v, cache_logf, page_table, l):
    B, T, H, dh = q.shape
    kp = cache_k[l, page_table]
    P = kp.shape[1] * kp.shape[2]
    kp = kp.reshape(B, P, H, dh).astype(jnp.float32)
    vp = cache_v[l, page_table].reshape(B, P, H, dh).astype(jnp.float32)
    lfp = cache_logf[l, page_table].reshape(B, P, H).astype(jnp.float32)
    Ft = jnp.swapaxes(jnp.cumsum(jnp.concatenate([lfp, lf], axis=1), axis=1), 1, 2)
    Fq = Ft[:, :, P:]
    scale = DH_C ** -0.5
    s_past = jnp.einsum("bqhd,bphd->bhqp", q, kp) * scale + Fq[..., None] - Ft[:, :, None, :P]
    s_new = jnp.einsum("bqhd,bkhd->bhqk", q, k) * scale + Fq[..., None] - Ft[:, :, None, P:]
    s_new = jnp.where(jnp.tril(jnp.ones((T, T), dtype=bool)), s_new, -jnp.inf)
    p = jax.nn.softmax(jnp.concatenate([s_past, s_new], axis=-1), axis=-1)
    return jnp.einsum("bhqp,bphd->bqhd", p[..., :P], vp) + jnp.einsum("bhqk,bkhd->bqhd", p[..., P:], v)

def trunk_layer(l, x, c, samp, W):
    (w_ada, b_ada, g_norm1, g_norm2, w_in, b_in, g_head_a, w_pool, s_pool, w_out, w_up, w_down) = W
    f32 = jnp.float32
    B, T, _ = x.shape
    mod = jax.nn.silu(c.astype(f32)) @ w_ada[l].astype(f32) + b_ada[l].astype(f32)
    sh1, sc1, g1, sh2, sc2, g2 = jnp.split(mod[:, None, :], 6, axis=-1)
    h = (rmsnorm(x, g_norm1[l]) * (1.0 + sc1) + sh1).astype(x.dtype)
    p = (h @ w_in[l] + b_in[l]).astype(f32)
    qa, ka, va, ia, fa, oa, u, qc, kc, vc, fc = split_cols(p)
    if samp is None:
        C0 = jnp.zeros((B, H_A, DV_A, DK_A), f32)
        n0 = jnp.zeros((B, H_A, DK_A), f32)
        m0 = jnp.zeros((B, H_A), f32)
        hist = jnp.zeros((B, POOL_HIST, W_B), f32)
        pos0 = 0
    else:
        cache_k, cache_v, cache_logf, page_table, state_C, state_n, state_m, state_pool = samp
        C0 = state_C[l].astype(f32)
        n0 = state_n[l].astype(f32)
        m0 = state_m[l].astype(f32)
        hist = state_pool[l].astype(f32)
        pos0 = page_table.shape[1] * cache_k.shape[2]
    ha, C1, n1, m1 = mlstm(qa.reshape(B, T, H_A, DK_A), ka.reshape(B, T, H_A, DK_A) * (DK_A ** -0.5),
                           va.reshape(B, T, H_A, DV_A), ia, fa, C0, n0, m0)
    ha = ha * lax.rsqrt(jnp.mean(ha * ha, axis=-1, keepdims=True) + EPS) * g_head_a[l].astype(f32)
    ha = jax.nn.sigmoid(oa) * ha.reshape(B, T, W_A)
    hb, hist1 = pool_mix(u, hist, pos0, w_pool[l].astype(f32), s_pool[l].astype(f32))
    q_c = qc.reshape(B, T, H_C, DH_C)
    k_c = kc.reshape(B, T, H_C, DH_C)
    v_c = vc.reshape(B, T, H_C, DH_C)
    lf = jax.nn.log_sigmoid(fc)
    if samp is None:
        hc = fox_prompt(q_c, k_c, v_c, lf)
    else:
        hc = fox_sample(q_c, k_c, v_c, lf, cache_k, cache_v, cache_logf, page_table, l)
    mix = jnp.concatenate([ha, hb, hc.reshape(B, T, W_C)], axis=-1).astype(x.dtype) @ w_out[l]
    x = (x + g1 * mix).astype(x.dtype)
    h2 = (rmsnorm(x, g_norm2[l]) * (1.0 + sc2) + sh2).astype(x.dtype)
    ff = jnp.square(jax.nn.relu(h2 @ w_up[l])) @ w_down[l]
    x = (x + g2 * ff).astype(x.dtype)
    new = (k_c.astype(x.dtype), v_c.astype(x.dtype), lf.astype(x.dtype), C1, n1, m1, hist1)
    return x, new

def setup_inputs(seed: int = 0) -> dict:
    key = jax.random.key(seed)
    ks = jax.random.split(key, 26)
    f32 = jnp.float32

    def nrm(k, shape, s):
        return jax.random.normal(k, shape, f32) * s

    n_pages = PAST_LEN // PAGE_SIZE
    n_phys = (5 * DEC_BATCH * n_pages + 3) // 4
    page_table = jax.random.permutation(ks[0], n_phys)[:DEC_BATCH * n_pages].reshape(DEC_BATCH, n_pages).astype(jnp.int32)
    off_fa = col_offset(4)
    off_fc = col_offset(10)
    gate_off = jnp.zeros((N_IN,), f32)
    gate_off = gate_off.at[off_fa:off_fa + H_A].set(jnp.linspace(3.0, 6.0, H_A))
    gate_off = gate_off.at[off_fc:off_fc + H_C].set(FGATE_BIAS_C)
    return {
        "x_prompt": nrm(ks[1], (BATCH, SEQ, D_MODEL), 1.0),
        "x_sample": nrm(ks[2], (DEC_BATCH, DEC_SEQ, D_MODEL), 1.0),
        "c_prompt": nrm(ks[3], (BATCH, D_MODEL), 1.0),
        "c_sample": nrm(ks[4], (DEC_BATCH, D_MODEL), 1.0),
        "cache_k": nrm(ks[5], (DEPTH, n_phys, PAGE_SIZE, H_C, DH_C), 1.0),
        "cache_v": nrm(ks[6], (DEPTH, n_phys, PAGE_SIZE, H_C, DH_C), 1.0),
        "cache_logf": jax.nn.log_sigmoid(nrm(ks[7], (DEPTH, n_phys, PAGE_SIZE, H_C), 1.0) + FGATE_BIAS_C),
        "page_table": page_table,
        "state_C": nrm(ks[8], (DEPTH, DEC_BATCH, H_A, DV_A, DK_A), 0.1),
        "state_n": nrm(ks[9], (DEPTH, DEC_BATCH, H_A, DK_A), 0.1),
        "state_m": nrm(ks[10], (DEPTH, DEC_BATCH, H_A), 0.5),
        "state_pool": nrm(ks[11], (DEPTH, DEC_BATCH, POOL_HIST, W_B), 1.0),
        "w_ada": nrm(ks[12], (DEPTH, D_MODEL, 6 * D_MODEL), 0.5 * D_MODEL ** -0.5),
        "b_ada": nrm(ks[13], (DEPTH, 6 * D_MODEL), 0.02),
        "g_norm1": 1.0 + nrm(ks[14], (DEPTH, D_MODEL), 0.05),
        "g_norm2": 1.0 + nrm(ks[15], (DEPTH, D_MODEL), 0.05),
        "w_in": nrm(ks[16], (DEPTH, D_MODEL, N_IN), D_MODEL ** -0.5),
        "b_in": nrm(ks[17], (DEPTH, N_IN), 0.02) + gate_off[None, :],
        "g_head_a": 1.0 + nrm(ks[18], (DEPTH, H_A, DV_A), 0.05),
        "w_pool": nrm(ks[19], (DEPTH, G_B, CG_B, CG_B), CG_B ** -0.5),
        "s_pool": 1.0 + nrm(ks[20], (DEPTH, W_B), 0.1),
        "w_out": nrm(ks[21], (DEPTH, D_MIX, D_MODEL), D_MIX ** -0.5),
        "w_up": nrm(ks[22], (DEPTH, D_MODEL, D_FF), D_MODEL ** -0.5),
        "w_down": nrm(ks[23], (DEPTH, D_FF, D_MODEL), D_FF ** -0.5),
        "g_final": 1.0 + nrm(ks[24], (D_MODEL,), 0.05),
    }

def reference(x_prompt, x_sample, c_prompt, c_sample, cache_k, cache_v, cache_logf, page_table,
              state_C, state_n, state_m, state_pool, w_ada, b_ada, g_norm1, g_norm2, w_in, b_in,
              g_head_a, w_pool, s_pool, w_out, w_up, w_down, g_final):
    W = (w_ada, b_ada, g_norm1, g_norm2, w_in, b_in, g_head_a, w_pool, s_pool, w_out, w_up, w_down)
    samp = (cache_k, cache_v, cache_logf, page_table, state_C, state_n, state_m, state_pool)
    xp, xs = x_prompt, x_sample
    rows_p, rows_s = [], []
    for l in range(DEPTH):
        xp, sp = trunk_layer(l, xp, c_prompt, None, W)
        xs, ss = trunk_layer(l, xs, c_sample, samp, W)
        rows_p.append(sp)
        rows_s.append(ss)
    k_p, v_p, lf_p, C_p, n_p, m_p, pool_p = [jnp.stack(a) for a in zip(*rows_p)]
    k_s, v_s, lf_s, C_s, n_s, m_s, pool_s = [jnp.stack(a) for a in zip(*rows_s)]
    y_prompt = rmsnorm(xp, g_final).astype(x_prompt.dtype)
    y_sample = rmsnorm(xs, g_final).astype(x_sample.dtype)
    return (y_prompt, y_sample, k_p, v_p, lf_p, C_p, n_p, m_p, pool_p, k_s, v_s, lf_s, C_s, n_s, m_s, pool_s)


_drawn_inputs = setup_inputs


def setup_inputs(seed=0):
    import zlib

    import numpy as np

    out = dict(_drawn_inputs(seed))
    spreads = {}
    factors = {'cache_logf': 4.945, 'g_head_a': 8.0, 's_pool': 3.16}
    for name, (base, spread) in spreads.items():
        noise = np.random.default_rng([zlib.crc32(name.encode()), seed]).standard_normal(out[name].shape)
        drawn = base * np.exp(spread * noise) if base else spread * noise
        out[name] = __import__('jax').numpy.asarray(drawn.astype(out[name].dtype))
    for name, factor in factors.items():
        out[name] = (out[name] * factor).astype(out[name].dtype)
    return out
```

```python
import numpy as np
import concourse.bass as bass
from concourse import mybir
from concourse.alu_op_type import AluOpType as ALU

F32, F32R, I32 = mybir.dt.float32, mybir.dt.float32r, mybir.dt.int32
ACT = mybir.ActivationFunctionType
AXX = mybir.AxisListType.X

P = 128
LAYERS, DM, DFF = 2, 1024, 4096
SEQ, NB, NT = 1024, 8, 4
NS = NB * NT
TOK = SEQ + NS
NCH, CW = 3, TOK // 3
KT = DM // P
CH = SEQ // P
TT = CH + 1
HA, DK, DV = 4, 48, 96
HC, DH = 6, 64
HIST = 15
PAGES, PG = 16, 128
PAST = PAGES * PG
FF_GROUPS = DFF // DM
EPS = 1e-6
BIG = 1e30
QA, KA, OA, VA, U, QC, KC, VC, GT, NF = 0, 2, 4, 7, 10, 12, 15, 18, 21, 22
SH1, SC1, G1, SH2, SC2, G2 = range(0, 48, 8)


def columns(spec):
    at, out = 0, {}
    for name, n in spec:
        out[name] = slice(at, at + n)
        at += n
    return out, at


CONST, NCONST = columns([("ident", P), ("tri", P), ("ones", P), ("head", HC * P), ("pair", 2 * P), ("rep", 32),
                         ("block", NS), ("later", NT), ("batch", NB), ("count", 2 * 16), ("width", 2),
                         ("scale", NF), ("eps", 1)])
PARAM, NPARAM = columns([("b_in", NF), ("b_ada", 48), ("g1", KT), ("g2", KT), ("head", 3), ("pool", 2),
                         ("wpool", 2 * P), ("m0", NB)])


def trunk(nc, xT, cT, consts, params, g_final, w_ada, w_in, w_out, w_ff, state, hist, kT, v, lfT, pages,
          y, o_k, o_v, o_lf, o_C, o_m, o_Cs, o_ms, o_pool, o_pools, x_spill):
    at = [nc.sbuf_base + (-nc.sbuf_base) % 64]
    made = {}

    def region(n):
        a = at[0]
        at[0] += (n + 63) // 64 * 64
        assert at[0] <= nc.sbuf_usable_end, at[0]
        return a

    def tile(name, shape, offset, dt=F32):
        made[name] = made.get(name, 0) + 1
        assert made[name] == 1
        return nc.alloc_sbuf_tensor_at(name, shape, dt, offset=offset)

    ROW = TOK * 4
    con = tile("con", [P, NCONST], region(NCONST * 4))
    par = tile("par", [P, NPARAM], region(NPARAM * 4))
    mod = tile("mod", [P, 48, 9], region(48 * 9 * 4))
    cs = tile("cs", [P, KT, 9], region(KT * 9 * 4))
    gfin = tile("gfin", [P, KT], region(KT * 4))
    ptab = tile("ptab", [1, NB * PAGES], region(NB * PAGES * 4), I32)
    aH0, aL0 = region(KT * ROW), region(KT * ROW)
    F0 = region(NF * ROW)
    T0 = region(4 * ROW + 512)
    W0 = region(24576)
    assert T0 == F0 + NF * ROW
    aH = tile("aH", [P, KT, TOK], aH0, F32R)
    aL = tile("aL", [P, KT, TOK], aL0, F32R)
    mix = tile("mix", [P, KT, TOK], aL0)
    F = tile("F", [P, NF, TOK], F0)
    x = tile("x", [P, KT, TOK], F0)
    hH = tile("hH", [P, KT, TOK], F0 + KT * ROW, F32R)
    hL = tile("hL", [P, KT, TOK], F0 + 2 * KT * ROW, F32R)
    raw = [tile(f"raw{s}", [P, KT, P], W0 + 4096 * s) for s in range(2)]
    whi = [tile(f"whi{s}", [P, KT, P], W0 + 4096 * (2 + s), F32R) for s in range(2)]
    wlo = [tile(f"wlo{s}", [P, KT, P], W0 + 4096 * (4 + s), F32R) for s in range(2)]
    wada = [tile(f"wada{s}", [P, KT, 256], W0 + 8192 * s) for s in range(3)]
    work = [tile(f"work{s}", [P, TOK], W0 + ROW * s) for s in range(5)]
    ev = [tile(f"ev{s}", [P, TOK], T0 + ROW * r) for s, r in enumerate((2, 3, 0))]
    res = tile("res", [P, NB, NT], T0 + 4 * ROW)

    PS = nc.alloc_psum_tensor("PS", [P, 8, 512], F32)

    sems = []

    def sem(name):
        s = nc.alloc_semaphore(name)
        sems.append(s)
        return s

    def c(name, rows=P):
        return con[0:rows, CONST[name]]

    def pr(name):
        return par[:, PARAM[name]]

    ident = con[:, CONST["ident"]]

    def three(ap):
        return ap.rearrange("p (c n) -> p c n", c=NCH)

    def banks(s):
        return PS[:, 3 * s:3 * s + 3, 0:CW]

    def per_token(ap):
        n = ap.shape[0]
        return ap.rearrange("p (b o) -> p b o", o=1).to_broadcast([n, NB, NT])

    def chain_on(eng, done, base=0):
        n = [0]

        def link(ins):
            n[0] += 1
            ins.then_inc(done, 1)
            eng.wait_ge(done, base + n[0])
        return link

    i_in, i_sig, i_cs = sem("start_loaded"), sem("start_sigmoid"), sem("start_silu")
    with nc.Block() as block:
        @block.sync
        def _(sp):
            sp.dma_start(cs[:], cT).then_inc(i_in, 16)
            sp.dma_start(con[:], consts).then_inc(i_in, 16)
            sp.dma_start(gfin[:], g_final).then_inc(i_in, 16)
            sp.dma_start(ptab[:], pages).then_inc(i_in, 16)
            sp.dma_start(x[:], xT).then_inc(i_in, 16)
            sp.wait_ge(i_in, 80)

        @block.scalar
        def _(act):
            act.wait_ge(i_in, 80)
            nc.scalar.activation(work[0][:, 0:KT * 9], cs[:].rearrange("p a b -> p (a b)"), ACT.Sigmoid).then_inc(i_sig, 1)

        @block.vector
        def _(dve):
            dve.wait_ge(i_sig, 1)
            flat = cs[:].rearrange("p a b -> p (a b)")
            nc.vector.tensor_tensor(flat, flat, work[0][:, 0:KT * 9], ALU.mult).then_inc(i_cs, 1)

    def modulation(l):
        loaded = [sem(f"ada_loaded{s}") for s in range(3)]
        done, moved, lp = sem("ada_done"), sem("ada_moved"), sem("ada_params")
        N = 24
        with nc.Block() as block:
            @block.sync
            def _(sp):
                sp.dma_start(par[:], params[bass.ds(l, 1)].rearrange("a p n -> (a p) n")).then_inc(lp, 16)

                def load(i, s):
                    sp.dma_start(wada[s][:], w_ada[bass.ds(l * N + 3 * i + s, 1)].rearrange("a p k n -> (a p) k n"))\
                        .then_inc(loaded[s], 16)
                for s in range(3):
                    load(0, s)
                with sp.Fori(1, N // 3) as i:
                    for s in range(3):
                        sp.wait_ge(done, 3 * i + s - 2)
                        load(i, s)

            @block.tensor
            def _(pe):
                def panel(i, s):
                    pe.wait_ge(loaded[s], 16 * i + 16)
                    for n in range(2):
                        for k in range(KT):
                            last = nc.tensor.matmul(PS[:, 2 * s + n, 0:9], wada[s][:, k, n * P:(n + 1) * P], cs[:, k, :],
                                                    start=k == 0, stop=k == KT - 1)
                    last.then_inc(done, 1)
                for s in range(3):
                    panel(0, s)
                with pe.Fori(1, N // 3) as i:
                    for s in range(3):
                        pe.wait_ge(moved, 3 * i + s - 2)
                        panel(i, s)

            @block.vector
            def _(dve):
                dve.wait_ge(lp, 16)
                with dve.Fori(0, N // 3) as i:
                    for s in range(3):
                        dve.wait_ge(done, 3 * i + s + 1)
                        t = bass.ds(6 * i + 2 * s, 2)
                        b = pr("b_ada")[:, t].rearrange("p (a o) -> p a o", o=1).to_broadcast([P, 2, 9])
                        nc.vector.tensor_tensor(mod[:, t, :], PS[:, 2 * s:2 * s + 2, 0:9], b, ALU.add).then_inc(moved, 1)
                dve.wait_ge(moved, N)
                for sc, g in ((SC1, "g1"), (SC2, "g2")):
                    m = mod[:, sc:sc + KT, :]
                    b = pr(g).rearrange("p (a o) -> p a o", o=1).to_broadcast([P, KT, 9])
                    nc.vector.scalar_tensor_tensor(m, m, 1.0, b, ALU.add, ALU.mult).then_inc(moved, 1)
                dve.wait_ge(moved, N + 2)

    def rms(name, block, out):
        squared, summed, rooted = sem(f"{name}_squared"), sem(f"{name}_summed"), sem(f"{name}_rooted")

        def act_part(act):
            for k in range(KT):
                if k >= 2:
                    act.wait_ge(summed, k - 1)
                nc.scalar.activation(ev[k % 2][:], x[:, k, :], ACT.Square).then_inc(squared, 1)
            act.wait_ge(summed, KT)
            nc.scalar.activation(three(out), banks(0), ACT.Sqrt, bias=c("eps")).then_inc(rooted, 1)

        def pe_part(pe):
            for k in range(KT):
                pe.wait_ge(squared, k + 1)
                for n in range(NCH):
                    last = nc.tensor.matmul(PS[:, n, 0:CW], c("ones"), ev[k % 2][:, n * CW:(n + 1) * CW],
                                            start=k == 0, stop=k == KT - 1)
                last.then_inc(summed, 1)
        return act_part, pe_part, rooted

    def normalise(l, name, sc, sh, spill):
        chain, scaled, modded, high = (sem(f"{name}_{n}") for n in ("chain", "scaled", "modded", "high"))
        spilled, low = sem(f"{name}_spilled"), sem(f"{name}_low")
        rs = ev[2]
        with nc.Block() as block:
            act_rms, pe_rms, rooted = rms(name, block, rs[:])
            if spill:
                @block.sync
                def _(sp):
                    sp.dma_start(x_spill, x[:]).then_inc(spilled, 16)
                    sp.wait_ge(spilled, 16)

            @block.tensor
            def _(pe):
                pe_rms(pe)

            @block.scalar
            def _(act):
                act_rms(act)
                for k in range(KT):
                    t = work[k % 4]
                    act.wait_ge(scaled, k + 1)
                    nc.scalar.activation(t[:, 0:SEQ], t[:, 0:SEQ], ACT.Identity, scale=mod[:, sc + k, 0:1],
                                         bias=mod[:, sh + k, 0:1]).then_inc(modded, 1)

            @block.gpsimd
            def _(pool):
                for k in range(KT):
                    pool.wait_ge(modded, k + 1)
                    nc.gpsimd.tensor_copy(aH[:, k, :], work[k % 4][:]).then_inc(high, 1)

            @block.vector
            def _(dve):
                link = chain_on(dve, chain)
                dve.wait_ge(rooted, 1)
                link(nc.vector.reciprocal(rs[:], rs[:]))

                def take_low(k):
                    dve.wait_ge(high, k + 1)
                    nc.vector.tensor_tensor(aL[:, k, :], work[k % 4][:], aH[:, k, :].bitcast(F32), ALU.subtract).then_inc(low, 1)
                for k in range(KT):
                    t = work[k % 4]
                    if k >= 4:
                        dve.wait_ge(low, k - 3)
                    link(nc.vector.tensor_tensor(t[:], x[:, k, :], rs[:], ALU.mult))
                    s = t[:, SEQ:TOK].rearrange("p (b t) -> p b t", b=NB)
                    link(nc.vector.tensor_tensor(s, s, per_token(mod[:, sc + k, 1:9]), ALU.mult))
                    nc.vector.tensor_tensor(s, s, per_token(mod[:, sh + k, 1:9]), ALU.add).then_inc(scaled, 1)
                    if k >= 1:
                        take_low(k - 1)
                take_low(KT - 1)

    def stream(name, l, weights, n_panels):
        s = {"loaded": [sem(f"{name}_loaded{i}") for i in range(2)]}
        for n in ("high", "split", "done", "room", "chain", "chain_in"):
            s[n] = sem(f"{name}_{n}")

        def sync_part(sp):
            def load(i, p):
                sp.dma_start(raw[p][:], weights[bass.ds(l * n_panels + 2 * i + p, 1)].rearrange("a p k n -> (a p) k n"))\
                    .then_inc(s["loaded"][p], 16)
            for p in range(2):
                load(0, p)
            with sp.Fori(1, n_panels // 2) as i:
                for p in range(2):
                    sp.wait_ge(s["split"], 2 * i + p - 1)
                    load(i, p)

        def pool_part(pool):
            def split(i, p):
                pool.wait_ge(s["loaded"][p], 16 * i + 16)
                pool.sem_inc(s["chain_in"], 1)
                nc.gpsimd.tensor_copy(whi[p][:], raw[p][:]).then_inc(s["high"], 1)
                pool.wait_ge(s["high"], 2 * i + p + 1)
                nc.gpsimd.tensor_tensor(wlo[p][:], raw[p][:], whi[p][:].bitcast(F32), ALU.subtract).then_inc(s["split"], 1)
            for p in range(2):
                split(0, p)
            with pool.Fori(1, n_panels // 2) as i:
                for p in range(2):
                    pool.wait_ge(s["done"], 2 * i + p - 1)
                    split(i, p)
        return s, sync_part, pool_part

    def panel_product(p, high, low):
        for k in range(KT):
            for w, a in ((whi[p], high), (whi[p], low), (wlo[p], high)):
                for n in range(NCH):
                    last = nc.tensor.matmul(PS[:, 3 * p + n, 0:CW], w[:, k, :], a[:, k, n * CW:(n + 1) * CW],
                                            start=k == 0 and w is whi[p] and a is high,
                                            stop=k == KT - 1 and w is wlo[p])
        return last

    def add_residual(link, t, gate, j, last_sem):
        link(nc.vector.scalar_tensor_tensor(x[:, bass.ds(j, 1), 0:SEQ].rearrange("p a n -> p (a n)"), t[:, 0:SEQ],
                                            mod[:, bass.ds(gate + j, 1), 0:1].rearrange("p a n -> p (a n)"),
                                            x[:, bass.ds(j, 1), 0:SEQ].rearrange("p a n -> p (a n)"), ALU.mult, ALU.add))
        g = mod[:, bass.ds(gate + j, 1), 1:9].rearrange("p a n -> p (a n)")
        link(nc.vector.tensor_tensor(res[:], t[:, SEQ:TOK].rearrange("p (b t) -> p b t", b=NB), per_token(g), ALU.mult))
        xs = x[:, bass.ds(j, 1), SEQ:TOK].rearrange("p a (b t) -> p (a b) t", b=NB)
        nc.vector.tensor_tensor(xs, xs, res[:], ALU.add).then_inc(last_sem, 1)

    def projection(l):
        s, sync_part, pool_part = stream("in", l, w_in, NF)
        biased = sem("in_biased")
        with nc.Block() as block:
            block.sync(sync_part)
            block.gpsimd(pool_part)

            @block.tensor
            def _(pe):
                with pe.Fori(0, NF // 2) as i:
                    for p in range(2):
                        pe.wait_ge(s["split"], 2 * i + p + 1)
                        pe.wait_ge(s["room"], 2 * i + p + 1)
                        panel_product(p, aH, aL).then_inc(s["done"], 1)

            @block.vector
            def _(dve):
                nc.vector.tensor_tensor(pr("b_in"), pr("b_in"), c("scale"), ALU.mult).then_inc(biased, 1)

            @block.scalar
            def _(act):
                act.sem_inc(s["room"], 2)
                act.wait_ge(biased, 1)
                with act.Fori(0, NF // 2) as i:
                    for p in range(2):
                        j = 2 * i + p
                        act.wait_ge(s["done"], j + 1)
                        nc.scalar.activation(F[:, bass.ds(j, 1), :].rearrange("p a (c n) -> p (a c) n", c=NCH), banks(p),
                                             ACT.Identity, scale=con[:, bass.ds(CONST["scale"].start + j, 1)],
                                             bias=par[:, bass.ds(PARAM["b_in"].start + j, 1)]).then_inc(s["room"], 1)

    vA = tile("vA", [P, TT, HA, DV + 1], aH0)
    vC = tile("vC", [P, TT, HC * DH], aH0 + 13984)
    small0 = aH0 + 13984 + TT * HC * DH * 4
    cols = tile("cols", [P, TT, 3, HA], small0)
    CT = tile("CT", [P, HA, 97], small0 + 448)
    wK = tile("wK", [P, 2 * P], small0 + 2016)
    alast = tile("alast", [P, 2, CH + NB], small0 + 3040)
    small = tile("small", [P, 3, TT * HA], small0 + 3168)
    qz = [tile("qz0", [P, 2, 2, P], small0 + 3616), tile("qz1", [P, 2, 2, P], W0 + 5 * ROW)]
    qB = tile("qB", [P, HA, NB, NS], aL0 + 8192)
    LC = tile("LC", [P, TOK], T0)
    qs = tile("qs", [P, 2, TOK], T0 + ROW)
    E = [tile(f"E{s}", [P, 4 * P], T0 + 3 * ROW + 2048 * s) for s in range(2)]
    R3, Brow, arow, Mrow, mtrow = work
    num = tile("num", [P, TT, HA, 97], aL0 + 3 * ROW)
    C0 = tile("C0", [P, 2 * NB, 97], aL0 + 3 * ROW + 13984)
    wKb = tile("wKb", [P, NB, 2 * P], aL0)
    sq = tile("sq", [P, TT, HA, DV], W0)

    def rows_and_values(l):
        st, sc_, turned, moved, zeroed = (sem(f"rows_{n}") for n in ("store", "chain", "turned", "moved", "zeroed"))
        abs_done, stateful, exped, rowsdone = (sem(f"rows_{n}") for n in ("log", "state", "exp", "ready"))
        tr, bc, qdone = sem("rows_transposed"), sem("rows_broadcast"), sem("rows_q")
        sam = lambda t, r=HA: t[0:r, SEQ:TOK].rearrange("p (b t) -> p b t", b=NB)
        pro = lambda t, r=HA: t[0:r, 0:SEQ].rearrange("p (b t) -> p b t", b=CH)
        Z = F[:, GT, :]
        with nc.Block() as block:
            @block.sync
            def _(sp):
                sp.dma_start(C0[:], state[bass.ds(l, 1)].rearrange("a p b n -> (a p) b n")).then_inc(st, 16)
                sp.dma_start(o_k[bass.ds(l, 1)].rearrange("a p b n -> (a p) b n"), F[:, KC:KC + 3, :]).then_inc(st, 16)
                sp.dma_start(o_v[bass.ds(l, 1)].rearrange("a p b n -> (a p) b n"), F[:, VC:VC + 3, :]).then_inc(st, 16)
                sp.wait_ge(rowsdone, 2)
                sp.dma_start(o_lf[bass.ds(l, 1)].rearrange("a p n -> (a p) n"), LC[0:HC, :]).then_inc(st, 16)
                sp.dma_start(o_m[bass.ds(l, 1)].rearrange("a p n -> (a p) n"), mtrow[0:HA, SEQ - 1:SEQ]).then_inc(st, 16)
                with nc.allow_non_contiguous_dma(reason="32 values"):
                    sp.dma_start(o_ms[bass.ds(l, 1)].rearrange("a p n -> (a p) n"), sam(mtrow)[:, :, NT - 1]).then_inc(st, 16)
                sp.wait_ge(st, 96)

            @block.gpsimd
            def _(pool):
                nc.gpsimd.memset(R3[:], 0.0).then_inc(zeroed, 1)
                nc.gpsimd.memset(cols[:], 1.0).then_inc(zeroed, 1)
                nc.gpsimd.memset(vA[:], 1.0).then_inc(zeroed, 1)
                nc.gpsimd.memset(qB[:], 0.0).then_inc(zeroed, 1)
                nc.gpsimd.memset(num[:], 0.0).then_inc(zeroed, 1)
                nc.gpsimd.memset(CT[:], 0.0).then_inc(zeroed, 1)
                for z in qz:
                    nc.gpsimd.memset(z[:], 0.0).then_inc(zeroed, 1)

            @block.tensor
            def _(pe):
                for t in range(TT):
                    n = min(P, TOK - t * P)
                    for half, first in enumerate((VA, VC)):
                        i = 2 * t + half
                        if i >= 4:
                            pe.wait_ge(moved, i - 3)
                        for j in range(3):
                            last = nc.tensor.transpose(PS[0:n, i % 4, j * P:(j + 1) * P], F[:, first + j, t * P:t * P + n], ident)
                        last.then_inc(turned, 1)
                pe.wait_ge(rowsdone, 3)
                pe.wait_ge(exped, 3)
                pe.wait_ge(moved, 2 * TT)
                for t in range(TT):
                    n = min(P, TOK - t * P)
                    last = nc.tensor.transpose(PS[0:n, t // 4, (t % 4) * P:(t % 4 + 1) * P], R3[:, t * P:t * P + n], ident)
                last.then_inc(tr, 1)
                for j in range(2):
                    if j:
                        pe.wait_ge(qdone, 2)
                    for n in range(NCH):
                        last = nc.tensor.matmul(PS[:, 3 + n, 0:CW], c("pair", HA)[:, j * P:(j + 1) * P],
                                                arow[0:HA, n * CW:(n + 1) * CW], start=True, stop=True)
                    last.then_inc(bc, 1)

            @block.scalar
            def _(act):
                link = chain_on(act, abs_done)
                A = work[2]
                link(nc.scalar.activation(A[:], Z, ACT.Abs))
                link(nc.scalar.activation(A[:], A[:], ACT.Exp, scale=-1.0))
                link(nc.scalar.activation(A[:], A[:], ACT.Ln, bias=1.0))
                act.wait_ge(zeroed, 3)
                for t in range(TT):
                    n = min(P, TOK - t * P)
                    act.wait_ge(turned, 2 * t + 1)
                    nc.scalar.activation(vA[0:n, t, :, 0:DV], PS[0:n, (2 * t) % 4, 0:384].rearrange("p (h v) -> p h v", h=HA),
                                         ACT.Copy).then_inc(moved, 1)
                    act.wait_ge(turned, 2 * t + 2)
                    nc.scalar.activation(vC[0:n, t, :], PS[0:n, (2 * t + 1) % 4, 0:384], ACT.Copy).then_inc(moved, 1)
                act.wait_ge(rowsdone, 2)
                nc.scalar.activation(R3[64:64 + HA, :], mtrow[0:HA, :], ACT.Exp, scale=-1.0).then_inc(exped, 1)
                act.wait_ge(rowsdone, 3)
                nc.scalar.activation(R3[32:32 + HA, :], R3[32:32 + HA, :], ACT.Exp).then_inc(exped, 1)
                nc.scalar.activation(arow[0:HA, :], arow[0:HA, :], ACT.Exp).then_inc(exped, 1)
                act.wait_ge(tr, 1)
                for t in range(TT):
                    n = min(P, TOK - t * P)
                    src = PS[0:n, t // 4, (t % 4) * P:(t % 4 + 1) * P].rearrange("p (r q) -> p r q", r=4)[:, 0:3, 0:HA]
                    nc.scalar.activation(cols[0:n, t, :, :], src, ACT.Copy).then_inc(moved, 1)
                for k in range(3):
                    o = F[:, OA + k, :]
                    nc.scalar.activation(o, o, ACT.Sigmoid).then_inc(moved, 1)

            @block.vector
            def _(dve):
                link = chain_on(dve, sc_)
                dve.wait_ge(zeroed, 2)
                dve.wait_ge(abs_done, 3)
                A, lf = work[2], work[4]
                link(nc.vector.tensor_scalar(lf[:], Z, 0.0, None, ALU.min))
                link(nc.vector.tensor_tensor(lf[:], lf[:], A[:], ALU.subtract))
                nc.vector.tensor_copy(LC[0:HC, :], lf[64:64 + HC, :]).then_inc(rowsdone, 1)
                link(nc.vector.tensor_copy(arow[0:HA, :], lf[32:32 + HA, :]))
                link(nc.vector.memset(Mrow[0:HA, :], 1.0))
                link(nc.vector.tensor_tensor_scan(Brow[0:HA, 0:SEQ], Mrow[0:HA, 0:SEQ], arow[0:HA, 0:SEQ], 0.0, ALU.mult, ALU.add))
                link(nc.vector.tensor_copy(Brow[0:HA, SEQ:TOK], arow[0:HA, SEQ:TOK]))
                for t in range(1, NT):
                    b = sam(Brow)
                    link(nc.vector.tensor_tensor(b[:, :, t], b[:, :, t - 1], b[:, :, t], ALU.add))
                g = R3[0:HA, :]
                link(nc.vector.tensor_tensor(g, F[0:HA, GT, :], Brow[0:HA, :], ALU.subtract))
                link(nc.vector.tensor_tensor_scan(Mrow[0:HA, 0:SEQ], g[:, 0:SEQ], g[:, 0:SEQ], 0.0, ALU.max, ALU.max))
                m0 = par[0:HA, PARAM["m0"]]
                for t in range(NT):
                    before = m0 if t == 0 else sam(Mrow)[:, :, t - 1]
                    link(nc.vector.tensor_tensor(sam(Mrow)[:, :, t], before, sam(R3)[:, :, t], ALU.max))
                link(nc.vector.tensor_tensor(mtrow[0:HA, :], Brow[0:HA, :], Mrow[0:HA, :], ALU.add))
                def end(view, n, width):
                    return view[:, :, width - 1:width].to_broadcast([HA, n, width])
                w = R3[32:32 + HA, :]
                link(nc.vector.tensor_tensor(w[:, 0:SEQ].rearrange("p (b t) -> p b t", b=CH), pro(R3), end(pro(Mrow), CH, P), ALU.subtract))
                nc.vector.tensor_tensor(w[:, SEQ:TOK].rearrange("p (b t) -> p b t", b=NB), sam(R3), end(sam(Mrow), NB, NT),
                                        ALU.subtract).then_inc(rowsdone, 1)
                link(nc.vector.tensor_scalar(arow[0:HA, 0:P], Mrow[0:HA, 0:P], -1.0, None, ALU.mult))
                link(nc.vector.tensor_tensor(pro(arow)[:, 1:CH], pro(Mrow)[:, 0:CH - 1, P - 1:P].to_broadcast([HA, CH - 1, P]),
                                             pro(Mrow)[:, 1:CH], ALU.subtract))
                nc.vector.tensor_tensor(sam(arow), per_token(m0), sam(Mrow), ALU.subtract).then_inc(rowsdone, 1)
                dve.wait_ge(zeroed, 5)
                for j in range(2):
                    dve.wait_ge(bc, j + 1)
                    nc.vector.tensor_tensor(three(qs[:, j, :]), three(F[:, QA + j, :]), PS[:, 3:6, 0:CW], ALU.mult).then_inc(qdone, 1)
                    for ch in range(CH):
                        at_ = ch * P + P - 1
                        link(nc.vector.tensor_copy(alast[:, j, ch:ch + 1], PS[:, 3 + at_ // CW, at_ % CW:at_ % CW + 1]))
                    first = SEQ - 2 * CW
                    nc.vector.tensor_copy(alast[:, j, CH:CH + NB], PS[:, 5, first:first + NS].rearrange("p (b t) -> p b t", b=NB)[:, :, NT - 1])\
                        .then_inc(qdone, 1)
                dve.wait_ge(qdone, 4)
                for j in range(2):
                    for e in range(2):
                        for b in range(NB):
                            link(nc.vector.tensor_copy(qB[64 * e:64 * e + 64, 2 * j + e, b, b * NT:(b + 1) * NT],
                                                       qs[64 * e:64 * e + 64, j, SEQ + b * NT:SEQ + (b + 1) * NT]))

    def mlstm(l):
        SB, MB = (0, 5), (1, 6)
        names = ("query", "scores", "maxima", "clipped", "exp", "masked", "weighted", "chain", "out", "turned", "keys", "update", "state", "moved")
        S = {n: sem(f"mlstm_{n}") for n in names}
        st = sem("mlstm_store")
        units = [(ch, P) for ch in range(CH)] + [(CH, NS)]
        hp = lambda h: slice(64 * (h % 2), 64 * (h % 2) + 64)
        with nc.Block() as block:
            @block.tensor
            def _(pe):
                def begin(u):
                    ch, n = units[u]
                    t0 = ch * P
                    if u >= 2:
                        pe.wait_ge(S["weighted"], u - 1)
                    pe.wait_ge(S["query"], u + 1)
                    for j in range(2):
                        last = nc.tensor.matmul(PS[0:n, SB[u % 2], 2 * j * P:(2 * j + 2) * P], F[:, KA + j, t0:t0 + n],
                                                qz[u % 2][:, j].rearrange("p e t -> p (e t)"), start=True, stop=True)
                    last.then_inc(S["scores"], 1)
                    if u >= 2:
                        pe.wait_ge(S["clipped"], u - 1)
                    for h in range(HA):
                        last = nc.tensor.matmul(PS[0:n, MB[u % 2], h * P:h * P + n], con[0:HA, CONST["head"]][:, h * P:h * P + n],
                                                Mrow[0:HA, t0:t0 + n], start=True, stop=True)
                    last.then_inc(S["maxima"], 1)

                def finish(u):
                    ch, n = units[u]
                    t0 = ch * P
                    if u >= 1:
                        pe.wait_ge(S["keys"], u)
                    for j in range(2):
                        last = nc.tensor.transpose(PS[0:n, 3, j * P:(j + 1) * P], F[:, KA + j, t0:t0 + n], ident)
                    last.then_inc(S["turned"], 1)
                    pe.wait_ge(S["weighted"], u + 1)
                    if u >= 1:
                        pe.wait_ge(S["moved"], u)
                    if 1 <= u < CH:
                        pe.wait_ge(S["state"], u)
                    for h in range(HA):
                        out = PS[0:n, 2, h * 97:(h + 1) * 97]
                        more = [] if ch == 0 else [(qs[:, h // 2, t0:t0 + n], CT[:, h, :])] if ch < CH else \
                            [(qB[:, h, b, :], C0[:, 2 * b + h // 2, :]) for b in range(NB)]
                        last = nc.tensor.matmul(out, E[u % 2][0:n, h * P:h * P + n], vA[0:n, ch, h, :], start=True, stop=not more)
                        for i, (a, b) in enumerate(more):
                            last = nc.tensor.matmul(out, a, b, start=False, stop=i == len(more) - 1)
                    last.then_inc(S["out"], 1)
                    pe.wait_ge(S["keys"], u + 1)
                    if ch < CH:
                        for h in range(HA):
                            last = nc.tensor.matmul(PS[hp(h), 4, (h // 2) * 97:(h // 2 + 1) * 97], wK[0:n, h * 64:(h + 1) * 64],
                                                    vA[0:n, ch, h, :], start=True, stop=True, skip_group_check=True)
                        last.then_inc(S["update"], 1)
                    else:
                        for b in range(NB):
                            for h in range(HA):
                                i = 2 * b + h // 2
                                bank = (4, 5, 6, 7)[i // 4]
                                last = nc.tensor.matmul(PS[hp(h), bank, (i % 4) * 97:(i % 4 + 1) * 97], wKb[0:n, b, h * 64:(h + 1) * 64],
                                                        vA[0:n, ch, h, :], start=True, stop=True, skip_group_check=True)
                        last.then_inc(S["update"], 1)
                begin(0)
                for u in range(len(units)):
                    if u + 1 < len(units):
                        begin(u + 1)
                    if u == CH:
                        pe.wait_ge(S["state"], CH)
                    finish(u)

            @block.scalar
            def _(act):
                def query(u):
                    ch, n = units[u]
                    if u >= 2:
                        act.wait_ge(S["scores"], u - 1)
                    for e in range(2):
                        r = slice(64 * e, 64 * e + 64)
                        last = nc.scalar.activation(qz[u % 2][r, :, e, 0:n], F[r, QA:QA + 2, ch * P:ch * P + n], ACT.Copy)
                    last.then_inc(S["query"], 1)
                query(0)
                for u, (ch, n) in enumerate(units):
                    if u + 1 < len(units):
                        query(u + 1)
                    act.wait_ge(S["clipped"], u + 1)
                    v_ = E[u % 2][0:n, :].rearrange("p (h t) -> p h t", h=HA)[:, :, 0:n]
                    nc.scalar.activation(v_, v_, ACT.Exp, scale=-1.0).then_inc(S["exp"], 1)
                    act.wait_ge(S["out"], u + 1)
                    nc.scalar.activation(num[0:n, ch, :, :], PS[0:n, 2, 0:4 * 97].rearrange("p (h v) -> p h v", h=HA), ACT.Copy)\
                        .then_inc(S["moved"], 1)

            @block.gpsimd
            def _(pool):
                for u, (ch, n) in enumerate(units):
                    pool.wait_ge(S["exp"], u + 1)
                    v_ = E[u % 2][0:n, :].rearrange("p (h t) -> p h t", h=HA)[:, :, 0:n]
                    nc.gpsimd.affine_select(out=v_, in_=v_, compare_op=ALU.is_ge, fill=0.0, base=0,
                                            pattern=[[0, HA], [1, n]], channel_multiplier=-1).then_inc(S["masked"], 1)

            @block.vector
            def _(dve):
                link = chain_on(dve, S["chain"])
                for u, (ch, n) in enumerate(units):
                    if u >= 2:
                        dve.wait_ge(S["out"], u - 1)
                    dve.wait_ge(S["maxima"], u + 1)
                    for h in range(HA):
                        last = nc.vector.tensor_scalar(E[u % 2][0:n, h * P:h * P + n], PS[0:n, MB[u % 2], h * P:h * P + n],
                                                       cols[0:n, ch, 0, h:h + 1], 0.0, ALU.subtract, ALU.max)
                    last.then_inc(S["clipped"], 1)
                    dve.wait_ge(S["turned"], u + 1)
                    if u >= 1:
                        dve.wait_ge(S["update"], u)
                    for h in range(HA):
                        last = nc.vector.tensor_scalar(wK[0:n, h * 64:(h + 1) * 64], PS[0:n, 3, h * 64:(h + 1) * 64],
                                                       cols[0:n, ch, 1, h:h + 1], None, ALU.mult)
                    if ch == CH:
                        link(last)
                        k_ = wK[0:n, :].rearrange("p (o k) -> p o k", o=1).to_broadcast([n, NB, 2 * P])
                        m_ = con[0:n, CONST["batch"]].rearrange("p (b o) -> p b o", o=1).to_broadcast([n, NB, 2 * P])
                        last = nc.vector.tensor_tensor(wKb[0:n], k_, m_, ALU.mult)
                    last.then_inc(S["keys"], 1)
                    dve.wait_ge(S["masked"], u + 1)
                    dve.wait_ge(S["scores"], u + 1)
                    v_ = E[u % 2][0:n, :].rearrange("p (h t) -> p h t", h=HA)[:, :, 0:n]
                    if ch == CH:
                        m_ = con[0:n, CONST["block"]].rearrange("p (o t) -> p o t", o=1).to_broadcast([n, HA, NS])
                        link(nc.vector.tensor_tensor(v_, v_, m_, ALU.mult))
                    s_ = PS[0:n, SB[u % 2], :].rearrange("p (h t) -> p h t", h=HA)[:, :, 0:n]
                    nc.vector.tensor_tensor(v_, v_, s_, ALU.mult).then_inc(S["weighted"], 1)
                    dve.wait_ge(S["update"], u + 1)
                    if ch < CH:
                        dve.wait_ge(S["out"], u + 1)
                        for h in range(HA):
                            j = h // 2
                            last = nc.vector.scalar_tensor_tensor(CT[hp(h), h, :], CT[hp(h), h, :], alast[hp(h), j, ch:ch + 1],
                                                                  PS[hp(h), 4, j * 97:(j + 1) * 97], ALU.mult, ALU.add)
                        last.then_inc(S["state"], 1)
                    else:
                        dve.wait_ge(S["out"], u + 1)
                        for b in range(NB):
                            for j in range(2):
                                i = 2 * b + j
                                last = nc.vector.scalar_tensor_tensor(C0[:, i, :], C0[:, i, :], alast[:, j, CH + b:CH + b + 1],
                                                                      PS[:, 4 + i // 4, (i % 4) * 97:(i % 4 + 1) * 97], ALU.mult, ALU.add)
                        last.then_inc(S["state"], 1)

            @block.sync
            def _(sp):
                sp.wait_ge(S["state"], CH)
                for e in range(2):
                    sp.dma_start(o_C[bass.ds(l, 1), 64 * e:64 * e + 64].rearrange("a p b n -> (a p) b n"),
                                 CT[64 * e:64 * e + 64].rearrange("p (b e) n -> p b e n", e=2)[:, :, e]).then_inc(st, 16)
                sp.wait_ge(S["state"], CH + 1)
                sp.dma_start(o_Cs[bass.ds(l, 1)].rearrange("a p b n -> (a p) b n"), C0[:]).then_inc(st, 16)
                sp.wait_ge(st, 48)

    def mlstm_out(l):
        chain, squared, rooted, ready, turned, joined = (sem(f"heads_{n}") for n in ("chain", "sum", "root", "ready", "turned", "joined"))
        s0, s1, s2 = small[:, 0, :], small[:, 1, :], small[:, 2, :]
        th = lambda a: a.rearrange("p (t h) -> p t h", t=TT)
        wide = lambda a: th(a).rearrange("p t (h o) -> p (t h) o", o=1).to_broadcast([P, TT * HA, DV])
        nv = num[:].rearrange("p t h v -> p (t h) v")
        with nc.Block() as block:
            @block.vector
            def _(dve):
                link = chain_on(dve, chain)
                den = nv[:, :, DV]
                link(nc.vector.scalar_tensor_tensor(s0, den, -1.0, den, ALU.mult, ALU.max))
                link(nc.vector.tensor_tensor(th(s0), th(s0), cols[:, :, 2, :], ALU.max))
                link(nc.vector.reciprocal(s1, s0))
                link(nc.vector.tensor_tensor(nv[:, :, 0:DV], nv[:, :, 0:DV], wide(s1), ALU.mult))
                sv = sq[:].rearrange("p t h v -> p (t h) v")
                link(nc.vector.tensor_tensor(sv, nv[:, :, 0:DV], nv[:, :, 0:DV], ALU.mult))
                nc.vector.tensor_reduce(s0, sv, axis=AXX, op=ALU.add).then_inc(squared, 1)
                dve.wait_ge(rooted, 1)
                link(nc.vector.reciprocal(s1, s2))
                nc.vector.tensor_tensor(sv, nv[:, :, 0:DV], wide(s1), ALU.mult).then_inc(ready, 1)
                for t in range(TT):
                    n = min(P, TOK - t * P)
                    dve.wait_ge(turned, t + 1)
                    for j in range(3):
                        last = nc.vector.scalar_tensor_tensor(mix[:, j, t * P:t * P + n], PS[:, t % 4, j * P:j * P + n],
                                                              par[:, PARAM["head"]][:, j:j + 1], F[:, OA + j, t * P:t * P + n],
                                                              ALU.mult, ALU.mult)
                    last.then_inc(joined, 1)

            @block.scalar
            def _(act):
                act.wait_ge(squared, 1)
                nc.scalar.activation(s2, s0, ACT.Sqrt, scale=1.0 / DV, bias=c("eps")).then_inc(rooted, 1)

            @block.tensor
            def _(pe):
                pe.wait_ge(ready, 1)
                for t in range(TT):
                    n = min(P, TOK - t * P)
                    if t >= 4:
                        pe.wait_ge(joined, t - 3)
                    for j in range(3):
                        last = nc.tensor.transpose(PS[:, t % 4, j * P:j * P + n],
                                                   sq[0:n, t].rearrange("p h v -> p (h v)")[:, j * P:(j + 1) * P], ident[0:n, 0:n])
                    last.then_inc(turned, 1)

    w2, w4, w8 = work[0], work[1], work[2]
    ubar = tile("ubar", [P, 2, TOK], T0 + ROW)
    ext = tile("ext", [P, 2, NB, HIST + NT], W0 + 3 * ROW)
    e2 = [tile(f"e{i}", [P, NB, HIST + NT], W0 + 3 * ROW + 1280 + 640 * i) for i in range(4)]
    tail = tile("tail", [P, 2, HIST], W0 + 3 * ROW + 1280 + 4 * 640)

    def pooling(l):
        ld, chain, ready, prod, moved, st = (sem(f"pool_{n}") for n in ("loaded", "chain", "ready", "product", "moved", "store"))
        with nc.Block() as block:
            @block.sync
            def _(sp):
                with nc.allow_non_contiguous_dma(reason="rows of 15"):
                    for j in range(2):
                        sp.dma_start(ext[:, j, :, 0:HIST], hist[bass.ds(l, 1), :, j].rearrange("a p b n -> (a p) b n")).then_inc(ld, 16)
                sp.wait_ge(ready, 1)
                sp.dma_start(o_pool[bass.ds(l, 1)].rearrange("a p b n -> (a p) b n"), tail[:]).then_inc(st, 16)
                for j in range(2):
                    sp.dma_start(o_pools[bass.ds(l, 1), :, j].rearrange("a p b n -> (a p) b n"), ext[:, j, :, NT:NT + HIST]).then_inc(st, 16)
                sp.wait_ge(st, 48)

            @block.vector
            def _(dve):
                link = chain_on(dve, chain)
                dve.wait_ge(ld, 32)
                for j in range(2):
                    link(nc.vector.tensor_copy(ext[:, j, :, HIST:], F[:, U + j, SEQ:TOK].rearrange("p (b t) -> p b t", b=NB)))
                nc.vector.tensor_copy(tail[:], F[:, U:U + 2, SEQ - HIST:SEQ]).then_inc(ready, 1)

                def window(dst, src, step, rows, n):
                    link(nc.vector.tensor_copy(dst[rows, 0:step], src[rows, 0:step]))
                    link(nc.vector.tensor_tensor(dst[rows, step:n], src[rows, step:n], src[rows, 0:n - step], ALU.add))

                def window_ext(dst, src, step, first, rows):
                    link(nc.vector.tensor_tensor(dst[rows, :, first:], src[rows, :, first:], src[rows, :, first - step:HIST + NT - step], ALU.add))

                for j in range(2):
                    u, ue = F[:, U + j, :], ext[:, j]
                    every, lower, upper = slice(0, P), slice(0, 64), slice(64, P)
                    window(w2, u, 1, every, SEQ)
                    window_ext(e2[0], ue, 1, 1, every)
                    if j == 0:
                        window(w4, w2, 2, upper, SEQ)
                        window_ext(e2[1], e2[0], 2, 3, upper)
                        parts = [(lower, w2, e2[0]), (upper, w4, e2[1])]
                    else:
                        window(w4, w2, 2, every, SEQ)
                        window_ext(e2[1], e2[0], 2, 3, every)
                        window(w8, w4, 4, every, SEQ)
                        window_ext(e2[2], e2[1], 4, 7, every)
                        window(w2, w8, 8, upper, SEQ)
                        window_ext(e2[3], e2[2], 8, 15, upper)
                        parts = [(lower, w8, e2[2]), (upper, w2, e2[3])]
                    for rows, s, se in parts:
                        wd = con[rows, CONST["width"]][:, j:j + 1]
                        cnt = con[rows, CONST["count"]][:, 16 * j:16 * j + 16]
                        link(nc.vector.tensor_tensor(s[rows, 0:16], s[rows, 0:16], cnt, ALU.mult))
                        link(nc.vector.scalar_tensor_tensor(ubar[rows, j, 0:SEQ], s[rows, 0:SEQ], wd, u[rows, 0:SEQ], ALU.mult, ALU.subtract))
                        link(nc.vector.scalar_tensor_tensor(ubar[rows, j, SEQ:TOK].rearrange("p (b t) -> p b t", b=NB),
                                                            se[rows, :, HIST:], wd, ue[rows, :, HIST:], ALU.mult, ALU.subtract))
                    dve.sem_inc(prod, 1)

            @block.tensor
            def _(pe):
                for j in range(2):
                    pe.wait_ge(prod, j + 1)
                    for n in range(NCH):
                        last = nc.tensor.matmul(PS[:, 3 * j + n, 0:CW], par[:, PARAM["wpool"]][:, j * P:(j + 1) * P],
                                                ubar[:, j, n * CW:(n + 1) * CW], start=True, stop=True)
                    last.then_inc(moved, 1)

            @block.scalar
            def _(act):
                for j in range(2):
                    act.wait_ge(moved, j + 1)
                    nc.scalar.activation(three(mix[:, 3 + j, :]), banks(j), ACT.Identity, scale=par[:, PARAM["pool"]][:, j:j + 1])

    Fb = tile("Fb", [P, HC, SEQ], W0)
    Trow = [tile(f"Trow{s}", [P, SEQ], T0 + ROW + 4096 * s) for s in range(2)]
    PT = [tile("PT0", [P, CH, P], T0 + ROW + 8192), tile("PT1", [P, CH, P], small0)]
    fo = F0
    Otok = tile("Otok", [P, HC * DH], fo)
    stats = tile("stats", [P, 3, 2], fo + 1536)
    Frow = tile("Frow", [P, SEQ], fo + 2048)
    onesr = tile("onesr", [P, SEQ], fo + 2048 + 4096)

    def fox_prompt(l):
        S = {n: sem(f"fox_{n}") for n in ("chain", "frow", "fb", "qk", "t", "exp", "turn", "pt", "pv", "o", "oturn", "omoved")}
        units = [(qb, h) for qb in range(CH) for h in range(HC)]
        NU = len(units)
        hp = lambda h: slice(64 * (h % 2), 64 * (h % 2) + 64)
        with nc.Block() as block:
            @block.tensor
            def _(pe):
                pe.wait_ge(S["frow"], 1)
                for h in range(HC):
                    for n in range(2):
                        i = 2 * h + n
                        if i >= 4:
                            pe.wait_ge(S["fb"], i - 3)
                        nc.tensor.matmul(PS[:, i % 4, :], con[0:HC, CONST["head"]][:, h * P:(h + 1) * P], Frow[0:HC, n * 512:(n + 1) * 512],
                                         start=True, stop=True).then_inc(S["turn"], 1)
                pe.wait_ge(S["fb"], 2 * HC)
                NF0 = 2 * HC
                for i in range(NU + 3):
                    if i < NU:
                        qb, h = units[i]
                        b = 2 * (i % 2)
                        if i >= 2:
                            pe.wait_ge(S["t"], i - 1)
                        n = (qb + 1) * P
                        for half in range((n + 511) // 512):
                            m = min(512, n - 512 * half)
                            diag = half == qb // 4
                            last = nc.tensor.matmul(PS[:, b + half, 0:m], F[hp(h), QC + h // 2, qb * P:(qb + 1) * P],
                                                    F[hp(h), KC + h // 2, 512 * half:512 * half + m], start=True, stop=not diag)
                            if diag:
                                last = nc.tensor.matmul(PS[:, b + half, m - P:m], ident, c("tri"), start=False, stop=True)
                        last.then_inc(S["qk"], 1)
                    if 0 <= i - 1 < NU:
                        u = i - 1
                        qb, h = units[u]
                        pe.wait_ge(S["exp"], u + 1)
                        if u >= 1:
                            pe.wait_ge(S["pt"], u)
                        for k in range(qb + 1):
                            last = nc.tensor.transpose(PS[:, 4 + k // 4, (k % 4) * P:(k % 4 + 1) * P],
                                                       Trow[u % 2][:, k * P:(k + 1) * P], ident)
                        last.then_inc(S["turn"], 1)
                    if 0 <= i - 2 < NU:
                        u = i - 2
                        qb, h = units[u]
                        pe.wait_ge(S["pt"], u + 1)
                        if u >= 1:
                            pe.wait_ge(S["o"], u)
                        for k in range(qb + 1):
                            last = nc.tensor.matmul(PS[:, 6, 0:DH], PT[u % 2][:, k, :], vC[:, k, h * DH:(h + 1) * DH],
                                                    start=k == 0, stop=k == qb)
                        last.then_inc(S["pv"], 1)
                    if 0 <= i - 3 < NU and units[i - 3][1] == HC - 1:
                        qb = units[i - 3][0]
                        pe.wait_ge(S["o"], i - 2)
                        if qb:
                            pe.wait_ge(S["omoved"], qb)
                        for j in range(3):
                            last = nc.tensor.transpose(PS[:, 7, j * P:(j + 1) * P], Otok[:, j * P:(j + 1) * P], ident)
                        last.then_inc(S["oturn"], 1)

            @block.vector
            def _(dve):
                link = chain_on(dve, S["chain"])
                link(nc.vector.memset(onesr[0:HC, :], 1.0))
                nc.vector.tensor_tensor_scan(Frow[0:HC, :], onesr[0:HC, :], LC[0:HC, 0:SEQ], 0.0, ALU.mult, ALU.add).then_inc(S["frow"], 1)
                dve.wait_ge(S["fb"], 2 * HC)
                for i in range(NU + 2):
                    if i < NU:
                        qb, h = units[i]
                        n = (qb + 1) * P
                        b = 2 * (i % 2)
                        dve.wait_ge(S["qk"], i + 1)
                        if i >= 2:
                            dve.wait_ge(S["turn"], 2 * HC + i - 1)
                        nc.vector.tensor_tensor_reduce(out=Trow[i % 2][:, 0:n], in0=Fb[:, h, 0:n], in1=PS[:, b:b + 2, :].rearrange("p a n -> p (a n)")[:, 0:n],
                                                       scale=1.0, scalar=3.0e38, op0=ALU.add, op1=ALU.min,
                                                       accum_out=stats[:, 0, i % 2:i % 2 + 1]).then_inc(S["t"], 1)
                    if 0 <= i - 2 < NU:
                        u = i - 2
                        qb, h = units[u]
                        dve.wait_ge(S["pv"], u + 1)
                        if h == 0 and qb:
                            dve.wait_ge(S["oturn"], qb)
                        link(nc.vector.reciprocal(stats[:, 2, u % 2:u % 2 + 1], inv[u % 4][:]))
                        nc.vector.tensor_scalar(Otok[:, h * DH:(h + 1) * DH], PS[:, 6, 0:DH], stats[:, 2, u % 2:u % 2 + 1], None, ALU.mult)\
                            .then_inc(S["o"], 1)

            @block.scalar
            def _(act):
                for i in range(2 * HC):
                    act.wait_ge(S["turn"], i + 1)
                    nc.scalar.activation(Fb[:, i // 2, (i % 2) * 512:(i % 2 + 1) * 512], PS[:, i % 4, :], ACT.Copy).then_inc(S["fb"], 1)
                for i in range(NU + 4):
                    if i < NU:
                        qb, h = units[i]
                        n = (qb + 1) * P
                        act.wait_ge(S["t"], i + 1)
                        if i >= 4:
                            act.wait_ge(S["o"], i - 3)
                        nc.scalar.activation(Trow[i % 2][:, 0:n], Trow[i % 2][:, 0:n], ACT.Exp, scale=-1.0,
                                             bias=stats[:, 0, i % 2:i % 2 + 1], accum_out=inv[i % 4][:]).then_inc(S["exp"], 1)
                    if 0 <= i - 1 < NU:
                        u = i - 1
                        n = units[u][0] + 1
                        act.wait_ge(S["turn"], 2 * HC + u + 1)
                        if u >= 2:
                            act.wait_ge(S["pv"], u - 1)
                        for a in range((n + 3) // 4):
                            m = min(4, n - 4 * a)
                            last = nc.scalar.activation(PT[u % 2][:, 4 * a:4 * a + m, :],
                                                        PS[:, 4 + a, 0:m * P].rearrange("p (k n) -> p k n", k=m), ACT.Copy)
                        last.then_inc(S["pt"], 1)
                    if 0 <= i - 4 < NU and units[i - 4][1] == HC - 1:
                        qb = units[i - 4][0]
                        act.wait_ge(S["oturn"], qb + 1)
                        nc.scalar.activation(mix[:, 5:8, qb * P:(qb + 1) * P], PS[:, 7, 0:384].rearrange("p (j n) -> p j n", j=3), ACT.Copy)\
                            .then_inc(S["omoved"], 1)

    inv = [tile(f"rowsum{i}", [P, 1], fo + 1536 + 64 + 32 * i) for i in range(4)]

    LFW = PAST + NT
    LF = tile("LF", [P, LFW], T0 + ROW)
    fo2 = F0
    Sc = tile("Sc", [P, LFW], fo2)
    PTs = tile("PTs", [P, PAGES, P], fo2 + 8256)
    ones2 = tile("ones2", [P, LFW], fo2 + 8256 + 8192)
    Qb = tile("Qb", [P, NB, 3, 32], fo2 + 8256 + 8192 + 8256)
    PN = tile("PN", [P, NS], fo2 + 27776)
    PTn = tile("PTn", [NS, P], fo2 + 27776 + 128)
    Os = tile("Os", [P, HC * DH], fo2 + 27776 + 640)
    st5 = tile("st5", [P, 8], fo2 + 27776 + 640 + 1536)
    Sn = tile("Sn", [P, NT], fo2 + 27776 + 640 + 1536 + 64)
    assert 27776 + 640 + 1536 + 128 <= 10 * ROW
    KR = 4
    Kp = [tile(f"Kp{i}", [P, 3, 4, PG], W0 + 6144 * i) for i in range(KR)]
    VRN = 8
    Vp = [tile(f"Vp{i}", [PG, HC * DH], fo2 + 30336 + 1536 * i) for i in range(VRN)]
    assert 30336 + 1536 * VRN <= 10 * ROW + 2 * ROW

    def fox_sample(l):
        S = {n: sem(f"past_{n}") for n in ("chain", "q", "lf", "f", "kdone", "t", "exp", "zero", "turn", "moved", "pn", "vdone", "o", "back", "out", "newf", "newp", "fnew", "snew")}
        kl = [sem(f"past_k{i}") for i in range(KR)]
        vl = [sem(f"past_v{i}") for i in range(VRN)]
        NG, QUADS = 2, PAGES // 4
        kunits = [(g, qd, b) for g in range(NG) for qd in range(QUADS) for b in range(4)]
        vunits = [(g, b, pg) for g in range(NG) for b in range(4) for pg in range(PAGES)]
        with nc.Block() as block:
            @block.sync
            def _(sp):
                ki = vi = 0
                for g in range(NG):
                    if g:
                        sp.wait_ge(S["exp"], g)
                    else:
                        sp.wait_ge(S["zero"], 1)
                    for b in range(4):
                        for pg in range(PAGES):
                            n = (4 * g + b) * PAGES + pg
                            page = sp.value_load(ptab[0:1, n:n + 1], min_val=0, max_val=kT.shape[1] - 1)
                            src = lfT[bass.ds(l, 1), bass.ds(page, 1)].rearrange("a c h (o n) -> (a c h) o n", o=1).to_broadcast([HC, NT, PG])
                            sp.dma_start(LF[32 * b:32 * b + HC * NT, pg * PG:(pg + 1) * PG], src).then_inc(S["lf"], 16)
                    for qd in range(QUADS):
                        for b in range(4):
                            if ki >= KR:
                                sp.wait_ge(S["kdone"], ki - KR + 1)
                            for k in range(4):
                                n = (4 * g + b) * PAGES + qd * 4 + k
                                page = sp.value_load(ptab[0:1, n:n + 1], min_val=0, max_val=kT.shape[1] - 1)
                                sp.dma_start(Kp[ki % KR][:, :, k, :], kT[bass.ds(l, 1), bass.ds(page, 1)].rearrange("a c p j n -> (a c p) j n"))\
                                    .then_inc(kl[ki % KR], 16)
                            ki += 1
                    for b in range(4):
                        for pg in range(PAGES):
                            if vi >= VRN:
                                sp.wait_ge(S["vdone"], vi - VRN + 1)
                            n = (4 * g + b) * PAGES + pg
                            page = sp.value_load(ptab[0:1, n:n + 1], min_val=0, max_val=kT.shape[1] - 1)
                            sp.dma_start(Vp[vi % VRN][:], v[bass.ds(l, 1), bass.ds(page, 1)].rearrange("a c p n -> (a c p) n")).then_inc(vl[vi % VRN], 16)
                            vi += 1

            @block.gpsimd
            def _(pool):
                nc.gpsimd.memset(LF[:], 0.0).then_inc(S["zero"], 1)
                nc.gpsimd.memset(PN[:], 0.0).then_inc(S["zero"], 1)

            @block.tensor
            def _(pe):
                ki = vi = 0
                pe.wait_ge(S["q"], 1)
                for g in range(NG):
                    if g:
                        pe.wait_ge(S["fnew"], g)
                        pe.wait_ge(S["back"], g)
                    for b in range(4):
                        last = nc.tensor.matmul(PS[32 * b:32 * b + 32, 6, 0:NT], con[0:HC, CONST["rep"]],
                                                LC[0:HC, SEQ + (4 * g + b) * NT:SEQ + (4 * g + b + 1) * NT], start=True, stop=True, skip_group_check=True)
                    last.then_inc(S["newf"], 1)
                    for b in range(4):
                        for j in range(3):
                            t0 = SEQ + (4 * g + b) * NT
                            last = nc.tensor.matmul(PS[32 * b:32 * b + 32, 7, 0:NT], Qb[:, 4 * g + b, j, :], F[:, KC + j, t0:t0 + NT],
                                                    start=j == 0, stop=j == 2, skip_group_check=True)
                    last.then_inc(S["snew"], 1)
                    for qd in range(QUADS):
                        if g * QUADS + qd >= 2:
                            pe.wait_ge(S["t"], g * QUADS + qd - 1)
                        for b in range(4):
                            pe.wait_ge(kl[ki % KR], 64 * (ki // KR + 1))
                            for j in range(3):
                                last = nc.tensor.matmul(PS[32 * b:32 * b + 32, qd % 2, :], Qb[:, 4 * g + b, j, :],
                                                        Kp[ki % KR][:, j].rearrange("p k n -> p (k n)"), start=j == 0, stop=j == 2, skip_group_check=True)
                            last.then_inc(S["kdone"], 1)
                            ki += 1
                    pe.wait_ge(S["exp"], g + 1)
                    pe.wait_ge(S["pn"], g + 1)
                    for a in range(4):
                        if g or a >= 2:
                            pe.wait_ge(S["moved"], 5 * g + max(a - 1, 0))
                        for k in range(4):
                            pg = 4 * a + k
                            last = nc.tensor.transpose(PS[:, 2 + a % 2, k * P:(k + 1) * P], Sc[:, pg * PG:(pg + 1) * PG], ident)
                        last.then_inc(S["turn"], 1)
                    pe.wait_ge(S["moved"], 5 * g + 3)
                    nc.tensor.transpose(PS[0:NS, 2, 0:P], PN[:], ident).then_inc(S["turn"], 1)
                    pe.wait_ge(S["moved"], 5 * g + 5)
                    for b in range(4):
                        out = PS[32 * b:32 * b + 32, 4, 0:HC * DH]
                        for pg in range(PAGES):
                            pe.wait_ge(vl[vi % VRN], 16 * (vi // VRN + 1))
                            nc.tensor.matmul(out, PTs[:, pg, 32 * b:32 * b + 32], Vp[vi % VRN][:], start=pg == 0, stop=False, skip_group_check=True)\
                                .then_inc(S["vdone"], 1)
                            vi += 1
                        last = nc.tensor.matmul(out, PTn[:, 32 * b:32 * b + 32], vC[0:NS, CH, :], start=False, stop=True, skip_group_check=True)
                    last.then_inc(S["o"], 1)
                    pe.wait_ge(S["out"], g + 1)
                    for j in range(3):
                        last = nc.tensor.transpose(PS[:, 5, j * P:(j + 1) * P], Os[:, j * P:(j + 1) * P], ident)
                    last.then_inc(S["newp"], 1)

            @block.vector
            def _(dve):
                link = chain_on(dve, S["chain"])
                link(nc.vector.memset(Qb[:], 0.0))
                link(nc.vector.memset(ones2[:], 1.0))
                for j in range(3):
                    for e in range(2):
                        r = slice(64 * e, 64 * e + 64)
                        h = 2 * j + e
                        last = nc.vector.tensor_copy(Qb[r, :, j, h * NT:(h + 1) * NT], F[r, QC + j, SEQ:TOK].rearrange("p (b t) -> p b t", b=NB))
                last.then_inc(S["q"], 1)
                dve.wait_ge(S["q"], 1)
                for g in range(NG):
                    dve.wait_ge(S["lf"], 16 * 64 * (g + 1))
                    dve.wait_ge(S["newf"], g + 1)
                    link(nc.vector.tensor_copy(LF[:, PAST:], PS[:, 6, 0:NT]))
                    link(nc.vector.tensor_tensor_scan(LF[:], ones2[:], LF[:], 0.0, ALU.mult, ALU.add))
                    if g:
                        dve.wait_ge(S["turn"], 5 * g)
                    dve.wait_ge(S["snew"], g + 1)
                    link(nc.vector.tensor_tensor(Sn[:], LF[:, PAST:], PS[:, 7, 0:NT], ALU.add))
                    dve.sem_inc(S["fnew"], 1)
                    link(nc.vector.tensor_tensor_reduce(out=Sc[:, PAST:], in0=Sn[:], in1=c("later"), scale=1.0, scalar=3.0e38,
                                                        op0=ALU.add, op1=ALU.min, accum_out=st5[:, 4:5]))
                    for qd in range(QUADS):
                        dve.wait_ge(S["kdone"], 4 * (g * QUADS + qd + 1))
                        nc.vector.tensor_tensor_reduce(out=Sc[:, qd * 512:(qd + 1) * 512], in0=LF[:, qd * 512:(qd + 1) * 512], in1=PS[:, qd % 2, :],
                                                       scale=1.0, scalar=3.0e38, op0=ALU.add, op1=ALU.min,
                                                       accum_out=st5[:, qd:qd + 1]).then_inc(S["t"], 1)
                    dve.wait_ge(S["t"], QUADS * (g + 1))
                    nc.vector.tensor_reduce(st5[:, 5:6], st5[:, 0:5], axis=AXX, op=ALU.min).then_inc(S["f"], 1)
                    dve.wait_ge(S["exp"], g + 1)
                    if g:
                        link(nc.vector.memset(PN[:, 0:16], 0.0))
                    for b in range(4):
                        r = slice(32 * b, 32 * b + 32)
                        t0 = (4 * g + b) * NT
                        link(nc.vector.tensor_copy(PN[r, t0:t0 + NT], Sc[r, PAST:]))
                    dve.sem_inc(S["pn"], 1)
                    link(nc.vector.reciprocal(st5[:, 7:8], st5[:, 6:7]))
                    dve.wait_ge(S["o"], g + 1)
                    nc.vector.tensor_scalar(Os[:], PS[:, 4, 0:HC * DH], st5[:, 7:8], None, ALU.mult).then_inc(S["out"], 1)
                    dve.wait_ge(S["newp"], g + 1)
                    for j in range(3):
                        for e in range(2):
                            h = 2 * j + e
                            r = slice(64 * e, 64 * e + 64)
                            src = PS[r, 5, j * P:(j + 1) * P].rearrange("p (b n) -> p b n", b=4)[:, :, h * NT:(h + 1) * NT]
                            last = nc.vector.tensor_copy(mix[r, 5 + j, SEQ + 16 * g:SEQ + 16 * g + 16].rearrange("p (b t) -> p b t", b=4), src)
                    last.then_inc(S["back"], 1)

            @block.scalar
            def _(act):
                act.wait_ge(S["zero"], 2)
                for g in range(NG):
                    act.wait_ge(S["f"], g + 1)
                    nc.scalar.activation(Sc[:], Sc[:], ACT.Exp, scale=-1.0, bias=st5[:, 5:6], accum_out=st5[:, 6:7]).then_inc(S["exp"], 1)
                    for a in range(4):
                        act.wait_ge(S["turn"], 5 * g + a + 1)
                        nc.scalar.activation(PTs[:, 4 * a:4 * a + 4, :], PS[:, 2 + a % 2, :].rearrange("p (k n) -> p k n", k=4), ACT.Copy).then_inc(S["moved"], 1)
                    act.wait_ge(S["turn"], 5 * g + 5)
                    nc.scalar.activation(PTn[:], PS[0:NS, 2, 0:P], ACT.Copy).then_inc(S["moved"], 1)

    def out_projection(l):
        s, sync_part, pool_part = stream("out", l, w_out, KT)
        reload, high, split, used = (sem(f"out_{n}") for n in ("x", "mix_high", "mix_split", "used"))
        with nc.Block() as block:
            @block.sync
            def _(sp):
                sp.dma_start(x[:], x_spill).then_inc(reload, 16)
                sync_part(sp)

            block.gpsimd(pool_part)

            @block.tensor
            def _(pe):
                pe.wait_ge(split, KT)
                with pe.Fori(0, KT // 2) as i:
                    for p in range(2):
                        pe.wait_ge(s["split"], 2 * i + p + 1)
                        pe.wait_ge(s["room"], 2 * i + p + 1)
                        panel_product(p, aH, aL).then_inc(s["done"], 1)

            @block.scalar
            def _(act):
                for k in range(KT):
                    nc.scalar.activation(aH[:, k, :], mix[:, k, :], ACT.Copy).then_inc(high, 1)
                act.sem_inc(s["room"], 2)
                evacuate(act, s, used, [(KT // 2, 0, ACT.Copy)], None)

            @block.vector
            def _(dve):
                for k in range(KT):
                    dve.wait_ge(high, k + 1)
                    nc.vector.tensor_tensor(aL[:, k, :], mix[:, k, :], aH[:, k, :].bitcast(F32), ALU.subtract).then_inc(split, 1)
                dve.sem_inc(used, 2)
                dve.wait_ge(reload, 16)
                with dve.Fori(0, KT // 2) as i:
                    for p in range(2):
                        dve.wait_ge(s["room"], 2 * i + p + 3)
                        link = chain_on(dve, s["chain"], (2 * i + p) * 2)
                        add_residual(link, ev[p], G1, 2 * i + p, used)

    def evacuate(act, s, used, runs, g):
        for pairs, first, func in runs:
            with act.Fori(0, pairs) as i:
                for p in range(2):
                    j = (first + 2 * i + p) if g is None else (16 * g + first + 2 * i + p)
                    act.wait_ge(s["done"], j + 1)
                    act.wait_ge(used, j + 1)
                    nc.scalar.activation(three(ev[p][:]), banks(p), func).then_inc(s["room"], 1)

    def mlp(l):
        s, sync_part, pool_part = stream("ff", l, w_ff, 2 * KT * FF_GROUPS)
        used, hidden, c2 = (sem(f"ff_{n}") for n in ("used", "hidden", "hidden_chain"))
        with nc.Block() as block:
            block.sync(sync_part)
            block.gpsimd(pool_part)

            @block.tensor
            def _(pe):
                with pe.Fori(0, FF_GROUPS) as g:
                    for first, (high, low) in ((0, (aH, aL)), (KT, (hH, hL))):
                        if first:
                            pe.wait_ge(hidden, KT * g + KT)
                            pe.sem_inc(s["chain_in"], 1)
                        with pe.Fori(0, KT // 2) as i:
                            for p in range(2):
                                j = 16 * g + first + 2 * i + p
                                pe.wait_ge(s["split"], j + 1)
                                pe.wait_ge(s["room"], j + 1)
                                panel_product(p, high, low).then_inc(s["done"], 1)

            @block.scalar
            def _(act):
                act.sem_inc(s["room"], 2)
                with act.Fori(0, FF_GROUPS) as g:
                    evacuate(act, s, used, [(KT // 2, 0, ACT.Relu), (KT // 2, KT, ACT.Copy)], g)

            @block.vector
            def _(dve):
                dve.sem_inc(used, 2)
                with dve.Fori(0, FF_GROUPS) as g:
                    with dve.Fori(0, KT // 2) as i:
                        for p in range(2):
                            j = 2 * i + p
                            t = ev[p][:]
                            dve.wait_ge(s["room"], 16 * g + j + 3)
                            link = chain_on(dve, c2, (KT * g + j) * 2)
                            link(nc.vector.tensor_tensor(t, t, t, ALU.mult))
                            H = hH[:, bass.ds(j, 1), :].rearrange("p a n -> p (a n)")
                            link(nc.vector.tensor_copy(H, t))
                            nc.vector.tensor_tensor(hL[:, bass.ds(j, 1), :].rearrange("p a n -> p (a n)"), t, H.bitcast(F32), ALU.subtract)\
                                .then_inc(hidden, 1)
                            dve.wait_ge(hidden, KT * g + j + 1)
                            dve.sem_inc(used, 1)
                    with dve.Fori(0, KT // 2) as i:
                        for p in range(2):
                            j = 2 * i + p
                            dve.wait_ge(s["room"], 16 * g + KT + j + 3)
                            link = chain_on(dve, s["chain"], (KT * g + j) * 2)
                            add_residual(link, ev[p], G2, j, used)


    def final(l):
        chain, scaled, stored, ready = (sem(f"final_{n}") for n in ("chain", "scaled", "stored", "ready"))
        rs = ev[2]
        with nc.Block() as block:
            act_rms, pe_rms, rooted = rms("final", block, rs[:])

            @block.tensor
            def _(pe):
                pe_rms(pe)

            @block.scalar
            def _(act):
                act_rms(act)

            @block.vector
            def _(dve):
                link = chain_on(dve, chain)
                dve.wait_ge(rooted, 1)
                link(nc.vector.reciprocal(rs[:], rs[:]))
                for k in range(KT):
                    if k >= 4:
                        dve.wait_ge(stored, 16 * (k - 3))
                    nc.vector.scalar_tensor_tensor(work[k % 4][:], x[:, k, :], gfin[:, k:k + 1], rs[:], ALU.mult, ALU.mult).then_inc(ready, 1)

            @block.sync
            def _(sp):
                for k in range(KT):
                    sp.wait_ge(ready, k + 1)
                    sp.dma_start(y[:, k, :], work[k % 4][:]).then_inc(stored, 16)
                    sp.wait_ge(stored, 16 * (k + 1))

    first = len(sems)
    with nc.Fori(0, RUN_LAYERS) as l:
        for stage in STAGES:
            {"modulation": modulation, "norm1": lambda l: normalise(l, "norm1", SC1, SH1, True), "projection": projection,
             "rows": rows_and_values, "mlstm": mlstm, "mlstm_out": mlstm_out, "pooling": pooling, "fox_prompt": fox_prompt,
             "fox_sample": fox_sample, "out": out_projection, "norm2": lambda l: normalise(l, "norm2", SC2, SH2, False),
             "mlp": mlp}[stage](l)
        with nc.Block() as block:
            @block.sync
            def _(sp):
                used = [s.num for s in sems[first:]]
                sp.sem_clear(range(min(used), max(used) + 1))
    if FINAL:
        final(0)


STAGES = ("modulation", "norm1", "projection", "rows", "mlstm", "mlstm_out", "pooling", "fox_prompt", "fox_sample", "out", "norm2", "mlp")
FINAL = True
RUN_LAYERS = LAYERS


def tiles_of(a, n_out):
    L, i, o = a.shape
    return a.reshape(L, i // P, P, o // n_out, n_out).transpose(0, 3, 2, 1, 4)


def feature_major(a):
    return a.reshape(a.shape[0], -1, P).transpose(2, 1, 0)


def input_columns():
    sizes = (HA * DK, HA * DK, HA * DV, HA, HA, HA * DV, 256, HC * DH, HC * DH, HC * DH, HC)
    off = np.concatenate([[0], np.cumsum(sizes)])
    idx = np.full(NF * P, -1)
    for h in range(HA):
        for t, o in ((QA, off[0]), (KA, off[1])):
            at = (t + h // 2) * P + 64 * (h % 2)
            idx[at:at + DK] = o + h * DK + np.arange(DK)
    for t, o, n in ((OA, 5, 384), (VA, 2, 384), (U, 6, 256), (QC, 7, 384), (KC, 8, 384), (VC, 9, 384)):
        idx[t * P:t * P + n] = off[o] + np.arange(n)
    for r, o, n in ((0, 3, HA), (32, 4, HA), (64, 10, HC)):
        idx[GT * P + r:GT * P + r + n] = off[o] + np.arange(n)
    return idx


def constants():
    c = np.zeros((P, NCONST), np.float32)
    p, n = np.arange(P)[:, None], np.arange(P)[None]
    c[:, CONST["ident"]] = p == n
    c[:, CONST["tri"]] = np.where(n > p, BIG, 0)
    c[:, CONST["ones"]] = 1.0 / DM
    for h in range(HC):
        c[h, CONST["head"].start + h * P:CONST["head"].start + (h + 1) * P] = 1
        c[h, CONST["rep"].start + h * NT:CONST["rep"].start + (h + 1) * NT] = 1
    for h in range(HA):
        at = CONST["pair"].start + (h // 2) * P + 64 * (h % 2)
        c[h, at:at + 64] = 1
    t = np.arange(NS)[None]
    c[:, CONST["block"]] = p // NT == t // NT
    c[:, CONST["later"]] = np.where(np.arange(NT)[None] > p % NT, BIG, 0)
    c[:, CONST["batch"]] = p // NT == np.arange(NB)[None]
    for j in range(2):
        w = np.where(p < 64, (2, 8)[j], (4, 16)[j])
        t = np.arange(16)[None]
        c[:, CONST["count"].start + 16 * j:CONST["count"].start + 16 * j + 16] = w / np.minimum(w, t + 1)
        c[:, CONST["width"].start + j] = 1 / w[:, 0]
    s = np.ones(NF)
    s[KA:KA + 2] = DK ** -0.5
    s[QC:QC + 3] = -DH ** -0.5
    c[:, CONST["scale"]] = s
    c[:, CONST["eps"]] = EPS
    return c


def kernel(**a):
    import concourse.bacc as bacc
    from concourse.bass_utils import run_bass_kernel_spmd

    a = {k: np.asarray(v) for k, v in a.items()}
    L = LAYERS
    rows = np.concatenate([a["x_prompt"].reshape(SEQ, DM), a["x_sample"].reshape(NS, DM)])
    idx = input_columns()
    w_in = np.zeros((L, DM, NF * P), np.float32)
    w_in[:, :, idx >= 0] = a["w_in"][:, :, idx[idx >= 0]]
    b_in = np.zeros((L, NF * P), np.float32)
    b_in[:, idx >= 0] = a["b_in"][:, idx[idx >= 0]]
    col = lambda v: v.reshape(L, -1, P).transpose(0, 2, 1)
    params = np.zeros((L, P, NPARAM), np.float32)
    for name, v in (("b_in", b_in), ("b_ada", a["b_ada"]), ("g1", a["g_norm1"]), ("g2", a["g_norm2"]),
                    ("head", a["g_head_a"].reshape(L, -1)), ("pool", a["s_pool"])):
        params[:, :, PARAM[name]] = col(v)
    for g in range(4):
        r, at = 64 * (g % 2), PARAM["wpool"].start + (g // 2) * P + 64 * (g % 2)
        params[:, r:r + 64, at:at + 64] = a["w_pool"][:, g]
    params[:, 0:HA, PARAM["m0"]] = a["state_m"].transpose(0, 2, 1)
    up = tiles_of(a["w_up"], P).reshape(L, FF_GROUPS, KT, P, KT, P)
    down = a["w_down"].reshape(L, FF_GROUPS, KT, P, KT, P).transpose(0, 1, 4, 3, 2, 5)
    w_ff = np.stack([up, down], axis=2)
    state = np.zeros((L, 2, 64, NB, 2, 97), np.float32)
    state[:, :, 0:DK, :, :, 0:DV] = a["state_C"].reshape(L, NB, 2, 2, DV, DK).transpose(0, 3, 5, 1, 2, 4)
    state[:, :, 0:DK, :, :, DV] = a["state_n"].reshape(L, NB, 2, 2, DK).transpose(0, 3, 4, 1, 2)
    hist = a["state_pool"].reshape(L, NB, HIST, 2, P).transpose(0, 4, 3, 1, 2)
    n_phys = a["cache_k"].shape[1]
    ins = {
        "xT": feature_major(rows), "cT": feature_major(np.concatenate([a["c_prompt"], a["c_sample"]])),
        "consts": constants(), "params": params, "g_final": a["g_final"].reshape(KT, P).T,
        "w_ada": tiles_of(a["w_ada"], 256).reshape(L * 24, P, KT, 256),
        "w_in": tiles_of(w_in, P).reshape(L * NF, P, KT, P), "w_out": tiles_of(a["w_out"], P).reshape(L * KT, P, KT, P),
        "w_ff": w_ff.reshape(L * 64, P, KT, P), "state": state.reshape(L, P, 2 * NB, 97), "hist": hist,
        "kT": a["cache_k"].reshape(L, n_phys, PG, 3, P).transpose(0, 1, 4, 3, 2),
        "v": a["cache_v"].reshape(L, n_phys, PG, HC * DH), "lfT": a["cache_logf"].transpose(0, 1, 3, 2),
        "pages": a["page_table"].reshape(1, -1),
    }
    outs = {
        "y": (P, KT, TOK), "o_k": (L, P, 3, TOK), "o_v": (L, P, 3, TOK), "o_lf": (L, HC, TOK), "o_C": (L, P, 2, 97),
        "o_m": (L, HA, 1), "o_Cs": (L, P, 2 * NB, 97), "o_ms": (L, HA, NB), "o_pool": (L, P, 2, HIST),
        "o_pools": (L, P, 2, NB, HIST), "x_spill": (P, KT, TOK),
    }
    nc = bacc.Bacc("TRN2", target_bir_lowering=False, num_devices=1)
    ins = {k: np.ascontiguousarray(v) for k, v in ins.items()}
    aps = [nc.dram_tensor(k, v.shape, mybir.dt.from_np(v.dtype), kind="ExternalInput").ap() for k, v in ins.items()]
    aps += [nc.dram_tensor(k, s, F32, kind="ExternalOutput" if k != "x_spill" else "Internal").ap() for k, s in outs.items()]
    trunk(nc, *aps)
    r = run_bass_kernel_spmd(nc, [ins], core_ids=[0]).results[0]

    def token_major(t, heads):
        t = np.moveaxis(t, -1, -3)
        t = np.swapaxes(t, -1, -2).reshape(t.shape[:-2] + heads)
        lead = t.shape[:-len(heads) - 1]
        n = len(lead)
        at = (slice(None),) * n
        return (t[at + (slice(0, SEQ),)].reshape(lead + (1, SEQ) + heads), t[at + (slice(SEQ, TOK),)].reshape(lead + (NB, NT) + heads))

    def states(t, nb):
        t = t.reshape(L, 2, 64, nb, 2, 97)[:, :, 0:DK].transpose(0, 3, 4, 1, 5, 2).reshape(L, nb, HA, 97, DK)
        return t[:, :, :, 0:DV], t[:, :, :, DV]

    yp, ys = token_major(r["y"], (DM,))
    kp, ks = token_major(r["o_k"], (HC, DH))
    vp, vs = token_major(r["o_v"], (HC, DH))
    lf = r["o_lf"].transpose(0, 2, 1)
    Cp, np_ = states(r["o_C"], 1)
    Cs, ns = states(r["o_Cs"], NB)
    pool = r["o_pool"].transpose(0, 3, 2, 1).reshape(L, 1, HIST, 256)
    pools = r["o_pools"].transpose(0, 3, 4, 2, 1).reshape(L, NB, HIST, 256)
    got = (yp, ys, kp, vp, lf[:, 0:SEQ].reshape(L, 1, SEQ, HC), Cp, np_, r["o_m"].reshape(L, 1, HA), pool,
           ks, vs, lf[:, SEQ:].reshape(L, NB, NT, HC), Cs, ns, r["o_ms"].transpose(0, 2, 1), pools)
    return tuple(np.ascontiguousarray(g) for g in got)
```
